# Optimizing a Trainium2 kernel written in Bass

```python
import jax, jax.numpy as jnp
from jax import lax
import numpy as np

D_MODEL = 1024
BATCH = 1
SEQ = 256
DEPTH = 2

GRID_W = 64
D_MIX = D_MODEL
D_ATTN = D_MIX // 2
N_HEADS = 8
HEAD_DIM = D_ATTN // N_HEADS
WIN_ROWS = 8
WIN_COLS = 16
D_POOL = D_MIX - D_ATTN
POOL_WINDOWS = (2, 4, 8, 16)
N_POOL_GROUPS = len(POOL_WINDOWS)
POOL_GROUP_DIM = D_POOL // N_POOL_GROUPS
D_IN_PROJ = 3 * D_ATTN + D_POOL
D_FF = 2816
RMS_EPS = 1e-6
NEG_INF = -1e30

kernel_name = "hybrid_natten_pool_macaron_block"

def rms_norm(x, g):
    xf = x.astype(jnp.float32)
    y = xf * lax.rsqrt(jnp.mean(xf * xf, axis=-1, keepdims=True) + RMS_EPS)
    return (y * g.astype(jnp.float32)).astype(x.dtype)

def swiglu(h, w_gate, w_up, w_down):
    return (jax.nn.silu(h @ w_gate) * (h @ w_up)) @ w_down

def neighborhood_attention(q, k, v, rpb):
    b, s, h, dh = q.shape
    rows = s // GRID_W
    kh = min(WIN_ROWS, rows)
    qg = q.reshape(b, rows, GRID_W, h, dh) * (dh ** -0.5)
    kg = k.reshape(b, rows, GRID_W, h, dh)
    vg = v.reshape(b, rows, GRID_W, h, dh)
    cols = jnp.arange(GRID_W)
    col_start = jnp.clip(cols - WIN_COLS // 2, 0, GRID_W - WIN_COLS)
    col_mask = (cols[None, :] >= col_start[:, None]) & (cols[None, :] < col_start[:, None] + WIN_COLS)
    dc_idx = jnp.clip(cols[None, :] - cols[:, None] + WIN_COLS - 1, 0, 2 * WIN_COLS - 2)
    rpb_f = rpb.astype(jnp.float32)

    def row_block(r):
        rs = jnp.clip(r - kh // 2, 0, rows - kh)
        q_r = lax.dynamic_index_in_dim(qg, r, axis=1, keepdims=False)
        k_r = lax.dynamic_slice_in_dim(kg, rs, kh, axis=1)
        v_r = lax.dynamic_slice_in_dim(vg, rs, kh, axis=1)
        dr_idx = rs + jnp.arange(kh) - r + WIN_ROWS - 1
        bias = rpb_f[:, dr_idx][:, :, dc_idx]
        bias = jnp.transpose(bias, (0, 2, 1, 3))
        scores = jnp.einsum("bqhd,bikhd->bhqik", q_r, k_r).astype(jnp.float32) + bias[None]
        scores = jnp.where(col_mask[None, None, :, None, :], scores, NEG_INF)
        probs = jax.nn.softmax(scores.reshape(b, h, GRID_W, kh * GRID_W), axis=-1)
        probs = probs.reshape(b, h, GRID_W, kh, GRID_W).astype(v.dtype)
        return jnp.einsum("bhqik,bikhd->bqhd", probs, v_r)

    out = lax.map(row_block, jnp.arange(rows))
    return jnp.transpose(out, (1, 0, 2, 3, 4)).reshape(b, s, h * dh)

def multiscale_pool(p, w_pool, scale):
    b, s, c = p.shape
    pf = p.astype(jnp.float32)
    csum = jnp.concatenate([jnp.zeros((b, 1, c), jnp.float32), jnp.cumsum(pf, axis=1)], axis=1)
    t = jnp.arange(s)
    outs = []
    for g, w in enumerate(POOL_WINDOWS):
        sl = slice(g * POOL_GROUP_DIM, (g + 1) * POOL_GROUP_DIM)
        lo = jnp.clip(t - w // 2, 0, s)
        hi = jnp.clip(t - w // 2 + w, 0, s)
        cg = csum[:, :, sl]
        mean = (cg[:, hi] - cg[:, lo]) / (hi - lo).astype(jnp.float32)[None, :, None]
        outs.append(mean - pf[:, :, sl])
    d = jnp.stack(outs, axis=2).astype(p.dtype)
    y = jnp.einsum("bsgc,gcd->bsgd", d, w_pool).reshape(b, s, c)
    return y * scale

def setup_inputs(seed: int = 0) -> dict:
    key = jax.random.key(seed)
    ks = jax.random.split(key, 20)
    f32 = jnp.float32

    def nrm(k, shape, fan_in):
        return jax.random.normal(k, shape, f32) * (fan_in ** -0.5)

    def gain(k, shape):
        return 1.0 + 0.05 * jax.random.normal(k, shape, f32)

    return {
        "x": jax.random.normal(ks[0], (BATCH, SEQ, D_MODEL), f32),
        "ffn1_norm": gain(ks[1], (DEPTH, D_MODEL)),
        "ffn1_w_gate": nrm(ks[2], (DEPTH, D_MODEL, D_FF), D_MODEL),
        "ffn1_w_up": nrm(ks[3], (DEPTH, D_MODEL, D_FF), D_MODEL),
        "ffn1_w_down": nrm(ks[4], (DEPTH, D_FF, D_MODEL), D_FF),
        "mix_norm": gain(ks[5], (DEPTH, D_MODEL)),
        "w_in": nrm(ks[6], (DEPTH, D_MODEL, D_IN_PROJ), D_MODEL),
        "rpb": 0.5 * jax.random.normal(ks[7], (DEPTH, N_HEADS, 2 * WIN_ROWS - 1, 2 * WIN_COLS - 1), f32),
        "w_pool": nrm(ks[8], (DEPTH, N_POOL_GROUPS, POOL_GROUP_DIM, POOL_GROUP_DIM), POOL_GROUP_DIM),
        "pool_scale": gain(ks[9], (DEPTH, D_POOL)),
        "w_out": nrm(ks[10], (DEPTH, D_MIX, D_MODEL), D_MIX),
        "ffn2_norm": gain(ks[11], (DEPTH, D_MODEL)),
        "ffn2_w_gate": nrm(ks[12], (DEPTH, D_MODEL, D_FF), D_MODEL),
        "ffn2_w_up": nrm(ks[13], (DEPTH, D_MODEL, D_FF), D_MODEL),
        "ffn2_w_down": nrm(ks[14], (DEPTH, D_FF, D_MODEL), D_FF),
        "final_norm": gain(ks[15], (D_MODEL,)),
    }

def reference(x, ffn1_norm, ffn1_w_gate, ffn1_w_up, ffn1_w_down, mix_norm, w_in, rpb,
              w_pool, pool_scale, w_out, ffn2_norm, ffn2_w_gate, ffn2_w_up, ffn2_w_down,
              final_norm):
    b, s, _ = x.shape
    for l in range(DEPTH):
        x = x + 0.5 * swiglu(rms_norm(x, ffn1_norm[l]), ffn1_w_gate[l], ffn1_w_up[l], ffn1_w_down[l])
        h = rms_norm(x, mix_norm[l])
        z = h @ w_in[l]
        q = z[..., 0:D_ATTN].reshape(b, s, N_HEADS, HEAD_DIM)
        k = z[..., D_ATTN:2 * D_ATTN].reshape(b, s, N_HEADS, HEAD_DIM)
        v = z[..., 2 * D_ATTN:3 * D_ATTN].reshape(b, s, N_HEADS, HEAD_DIM)
        p = z[..., 3 * D_ATTN:]
        a = neighborhood_attention(q, k, v, rpb[l])
        m = multiscale_pool(p, w_pool[l], pool_scale[l])
        x = x + jnp.concatenate([a, m], axis=-1) @ w_out[l]
        x = x + 0.5 * swiglu(rms_norm(x, ffn2_norm[l]), ffn2_w_gate[l], ffn2_w_up[l], ffn2_w_down[l])
    return rms_norm(x, final_norm)


_drawn_inputs = setup_inputs


def setup_inputs(seed=0):
    import zlib

    import numpy as np

    out = dict(_drawn_inputs(seed))
    spreads = {}
    factors = {}
    for name, (base, spread) in spreads.items():
        noise = np.random.default_rng([zlib.crc32(name.encode()), seed]).standard_normal(out[name].shape)
        drawn = base * np.exp(spread * noise) if base else spread * noise
        out[name] = __import__('jax').numpy.asarray(drawn.astype(out[name].dtype))
    for name, factor in factors.items():
        out[name] = (out[name] * factor).astype(out[name].dtype)
    return out
```

```python
from contextlib import ExitStack

import concourse.bass as bass
from concourse import mybir

D_MODEL = 1024
SEQ = 256
DEPTH = 2
GRID_W = 64
N_HEADS = 8
HEAD_DIM = 64
WIN_ROWS = 8
WIN_COLS = 16
D_ATTN = N_HEADS * HEAD_DIM
POOL_WINDOWS = (2, 4, 8, 16)
N_GROUPS = len(POOL_WINDOWS)
D_FF = 2816
RMS_EPS = 1e-6

P = 128
TT = SEQ // P
KT = D_MODEL // P
ROWS = SEQ // GRID_W
FC = 256
N_FF_CHUNKS = D_FF // FC
LAST = N_FF_CHUNKS - 1
UNIT = 2048
HALF = UNIT // 2
BANK = 512
SLOTS = 3
SCORE_BUFS = 4
DELTAS = ROWS + 2
STAGES = 3

FF1 = dict(g=(1, 2), d=0, stage=0)
FF2 = dict(g=(2, 0), d=1, stage=2)
MIX_SLOTS = [(2 + j) % SLOTS for j in range(12)]


def unit_counts():
    count = [0] * SLOTS
    before = []
    for stage in (FF1, None, FF2):
        before.append(tuple(count))
        if stage is None:
            for s in MIX_SLOTS:
                count[s] += 1
        else:
            count[stage["g"][0]] += N_FF_CHUNKS + 1
            count[stage["g"][1]] += N_FF_CHUNKS
            count[stage["d"]] += N_FF_CHUNKS - 1
    return before, tuple(count)


BEFORE, PER_LAYER = unit_counts()


def trunk(nc, x, ffn1_norm, ffn1_w_gate, ffn1_w_up, ffn1_w_down, mix_norm, w_in, rpb, w_pool,
          pool_scale, w_out, ffn2_norm, ffn2_w_gate, ffn2_w_up, ffn2_w_down, final_norm,
          identity, col_mask, pool_matrix, out):
    F32 = mybir.dt.float32
    F32R = mybir.dt.float32r
    ACT = mybir.ActivationFunctionType
    ALU = mybir.AluOpType

    ctx = ExitStack()
    with ctx:
        def sb(name, shape, dt=F32):
            return ctx.enter_context(nc.sbuf_tensor(name, shape, dt))

        def sem(name):
            return ctx.enter_context(nc.semaphore(name))

        w_raw = [sb(f"w_raw{s}", [P, UNIT]) for s in range(SLOTS)]
        w_hi = [sb(f"w_hi{s}", [P, UNIT], F32R) for s in range(SLOTS)]
        w_lo = [sb(f"w_lo{s}", [P, UNIT], F32R) for s in range(SLOTS)]
        resid = sb("resid", [P, TT, D_MODEL])
        normed = sb("normed", [P, TT, D_MODEL])
        xt_hi = sb("xt_hi", [P, TT, KT, P], F32R)
        xt_lo = sb("xt_lo", [P, TT, KT, P], F32R)
        gain = [sb(f"gain{j}", [P, D_MODEL]) for j in range(STAGES)]
        silu = sb("silu", [P, TT, FC])
        gated = sb("gated", [P, TT, FC])
        gt_hi = sb("gt_hi", [P, 2, 2, TT, P], F32R)
        gt_lo = sb("gt_lo", [P, 2, 2, TT, P], F32R)
        bias = sb("bias", [P, N_HEADS, DELTAS, GRID_W])
        mask = sb("mask", [P, GRID_W])
        z = sb("z", [P, TT, 4, 512])
        q_t = sb("q_t", [P, 4, TT, P])
        k_t = sb("k_t", [P, 4, TT, P])
        scores = sb("scores", [P, SCORE_BUFS, TT, SEQ])
        probs_t = sb("probs_t", [P, 2, TT, TT, P])
        pool_m = sb("pool_m", [P, TT, N_GROUPS, SEQ])
        w_pool_sb = sb("w_pool_sb", [P, N_GROUPS, P])
        pool_scale_sb = sb("pool_scale_sb", [P, N_GROUPS])
        ident = sb("ident", [P, P])
        wait_mark = sb("wait_mark", [P, 1])
        seeds = sb("seeds", [P, SLOTS + TT])
        zeros = sb("zeros", [P, BANK], F32R)
        mean_sq = sb("mean_sq", [P, TT])
        mean_eps = sb("mean_eps", [P, TT])
        eps = sb("eps", [P, 1])
        rstd = sb("rstd", [P, TT])
        minus_half = sb("minus_half", [P, 1])
        row_max = sb("row_max", [P, N_HEADS, TT])
        neg_max = sb("neg_max", [P, N_HEADS, TT])
        row_sum = sb("row_sum", [P, TT, N_HEADS])
        inv_sum = sb("inv_sum", [P, TT, N_HEADS])
        bias_dram = nc.dram_tensor("bias_scratch", [DEPTH, P, N_HEADS * DELTAS * GRID_W], F32,
                                   kind="Internal").ap()

        ps = ctx.enter_context(nc.psum_tensor("ps", [P, 8, BANK], F32))
        def acc(t, dh):
            return ps[:, 2 + 2 * t + dh, :]

        def heads_out(t):
            return z[:, t, 0, :]

        def diff_t(g):
            return z[:, g // 2, 1, (g % 2) * SEQ:(g % 2 + 1) * SEQ]

        raw_ready = [sem(f"raw_ready{s}") for s in range(SLOTS)]
        hi_ready = [sem(f"hi_ready{s}") for s in range(SLOTS)]
        lo_ready = [sem(f"lo_ready{s}") for s in range(SLOTS)]
        g0_used = sem("g0_used")
        down_used = sem("down_used")
        z_used = sem("z_used")
        w_out_used = sem("w_out_used")
        consts_loaded = sem("consts_loaded")
        x_loaded = sem("x_loaded")
        bias_rows_loaded = sem("bias_rows_loaded")
        gain0_loaded = sem("gain0_loaded")
        params_loaded = sem("params_loaded")
        bias_loaded = sem("bias_loaded")
        bias_masked = sem("bias_masked")
        zeros_ready = sem("zeros_ready")
        eps_ready = sem("eps_ready")
        final_gain_loaded = sem("final_gain_loaded")
        resid_ready = [sem(f"resid_ready{t}") for t in range(TT)]
        sq_ready = [sem(f"sq_ready{t}") for t in range(TT)]
        mean_ready = sem("mean_ready")
        rstd_ready = [sem(f"rstd_ready{t}") for t in range(TT)]
        normed_ready = sem("normed_ready")
        xt_ready = sem("xt_ready")
        xt_hi_ready = sem("xt_hi_ready")
        xt_lo_ready = sem("xt_lo_ready")
        gu_ready = [sem(f"gu_ready{t}") for t in range(TT)]
        silu_ready = [sem(f"silu_ready{t}") for t in range(TT)]
        gated_ready = [sem(f"gated_ready{t}") for t in range(TT)]
        gt_ready = sem("gt_ready")
        gt_hi_ready = sem("gt_hi_ready")
        gt_lo_ready = sem("gt_lo_ready")
        acc_ready = [sem(f"acc_ready{t}") for t in range(TT)]
        z_ready = sem("z_ready")
        z_qv_stored = sem("z_qv_stored")
        z_kp_stored = sem("z_kp_stored")
        qk_t_ready = sem("qk_t_ready")
        q_t_stored = sem("q_t_stored")
        k_t_stored = sem("k_t_stored")
        scores_ready = sem("scores_ready")
        biased_ready = sem("biased_ready")
        max_ready = sem("max_ready")
        probs_ready = sem("probs_ready")
        probs_t_ready = sem("probs_t_ready")
        probs_t_stored_a = sem("probs_t_stored_a")
        probs_t_stored_v = sem("probs_t_stored_v")
        pv_ready = sem("pv_ready")
        inv_ready = sem("inv_ready")
        heads_stored = sem("heads_stored")
        heads_t_ready = sem("heads_t_ready")
        heads_t_hi_ready = sem("heads_t_hi_ready")
        heads_t_lo_ready = sem("heads_t_lo_ready")
        diff_ready = sem("diff_ready")
        diff_stored = sem("diff_stored")
        pooled_ready = sem("pooled_ready")
        pooled_hi_ready = sem("pooled_hi_ready")
        pooled_lo_ready = sem("pooled_lo_ready")
        out_ready = sem("out_ready")
        out_stored = sem("out_stored")

        def unit_no(layer, stage, slot, k):
            return layer * PER_LAYER[slot] + (BEFORE[stage][slot] + k)

        def chunk_no(layer, ff, i):
            return layer * (2 * N_FF_CHUNKS) + ((ff["stage"] // 2) * N_FF_CHUNKS + i)

        def first_unit(layer, ff, a):
            return ff["g"][a], unit_no(layer, ff["stage"], ff["g"][a], 0)

        def down_no(layer, ff, i):
            return layer * (2 * LAST) + ((ff["stage"] // 2) * LAST + i)

        block = ctx.enter_context(nc.Block())

        @block.sync
        def _(sp):
            def wait_raw_free(slot, n):
                sp.wait_ge(lo_ready[slot], 2 * n + 1)

            def load_gate_up(layer, ff, weights, i, a):
                slot = ff["g"][a]
                wait_raw_free(slot, unit_no(layer, ff["stage"], slot, i))
                dst = w_raw[slot][:, :].rearrange("p (k m c) -> p k m c", k=4, m=2)
                for m, w in enumerate(weights[:2]):
                    src = w[bass.ds(layer, 1), a * 512:(a + 1) * 512, bass.ds(i * FC, FC)]
                    sp.dma_start(dst[:, :, m, :], src.rearrange("o (k p) c -> p (o k) c", p=P)
                                 ).then_inc(raw_ready[slot], 16)

            def load_down(layer, ff, weights, i, slot, k):
                wait_raw_free(slot, unit_no(layer, ff["stage"], slot, k))
                dst = w_raw[slot][:, :].rearrange("p (k c) -> p k c", k=2)
                for kt in range(2):
                    src = weights[2][bass.ds(layer, 1), bass.ds(i * FC + kt * P, P), :]
                    sp.dma_start(dst[:, kt, :], src.rearrange("o p c -> p (o c)")
                                 ).then_inc(raw_ready[slot], 16)

            def load_ff(layer, ff, weights):
                for i in range(2):
                    load_gate_up(layer, ff, weights, i, 0)
                    load_gate_up(layer, ff, weights, i, 1)
                load_down(layer, ff, weights, 0, ff["d"], 0)
                with sp.Fori(2, N_FF_CHUNKS) as i:
                    load_gate_up(layer, ff, weights, i, 0)
                    load_gate_up(layer, ff, weights, i, 1)
                    load_down(layer, ff, weights, i - 1, ff["d"], i - 1)
                load_down(layer, ff, weights, LAST, ff["g"][0], N_FF_CHUNKS)

            def load_mix(layer):
                for j, slot in enumerate(MIX_SLOTS):
                    wait_raw_free(slot, unit_no(layer, 1, slot, j // SLOTS))
                    if j < 8:
                        c, a = j // 2, j % 2
                        dst = w_raw[slot][:, :].rearrange("p (k c) -> p k c", k=4)
                        src = w_in[bass.ds(layer, 1), a * 512:(a + 1) * 512, c * 512:(c + 1) * 512]
                        src = src.rearrange("o (k p) c -> p (o k) c", p=P)
                        step = 2
                    else:
                        kt = (4, 6, 0, 2)[j - 8]
                        dst = w_raw[slot][:, :].rearrange("p (k c) -> p k c", k=2)
                        src = w_out[bass.ds(layer, 1), kt * P:(kt + 2) * P, :]
                        src = src.rearrange("o (k p) c -> p (o k) c", p=P)
                        step = 1
                    for h in (1, 0):
                        sp.dma_start(dst[:, h * step:(h + 1) * step, :],
                                     src[:, h * step:(h + 1) * step, :]
                                     ).then_inc(raw_ready[slot], 16)

            with sp.Fori(0, DEPTH) as layer:
                load_ff(layer, FF1, (ffn1_w_gate, ffn1_w_up, ffn1_w_down))
                load_mix(layer)
                load_ff(layer, FF2, (ffn2_w_gate, ffn2_w_up, ffn2_w_down))
            for t in range(TT):
                sp.wait_ge(out_ready, t + 1)
                sp.dma_start(out[0, t * P:(t + 1) * P, :], normed[:, t, :]).then_inc(out_stored, 16)
            sp.wait_ge(out_stored, 16 * TT)

        @block.gpsimd
        def _(pool):
            nc.gpsimd.memset(minus_half[:, :], -0.5)
            nc.gpsimd.memset(eps[:, :], RMS_EPS).then_inc(eps_ready, 1)
            rpb_row = 2 * WIN_COLS - 1
            rpb_head = (2 * WIN_ROWS - 1) * rpb_row
            dst = bias_dram.rearrange("l p (h e) -> l p h e", h=N_HEADS)
            for layer in range(DEPTH):
                for rq in range(P // GRID_W):
                    for h in range(N_HEADS):
                        first = ((layer * N_HEADS + h) * rpb_head
                                 + (WIN_ROWS - 3 - rq) * rpb_row + WIN_COLS - 1)
                        src = bass.AP(rpb.tensor, first, [[rpb_row, DELTAS], [-1, GRID_W], [1, GRID_W]])
                        pool.dma_start(
                            dst[layer, rq * GRID_W:(rq + 1) * GRID_W, h, :]
                            .rearrange("p (d c) -> d p c", d=DELTAS), src
                        ).then_inc(bias_rows_loaded, 16)

            def rstd_of(number):
                for t in range(TT):
                    pool.wait_ge(sq_ready[t], number + 1)
                    nc.gpsimd.tensor_tensor(mean_eps[:, t:t + 1], mean_sq[:, t:t + 1],
                                            eps[:, :], ALU.add).then_inc(mean_ready, 1)
                    pool.wait_ge(mean_ready, number * TT + (t + 1))
                    nc.gpsimd.tensor_tensor(rstd[:, t:t + 1], mean_eps[:, t:t + 1],
                                            minus_half[:, :], ALU.pow).then_inc(rstd_ready[t], 1)

            pool.wait_ge(eps_ready, 1)
            with pool.Fori(0, STAGES * DEPTH + 1) as number:
                rstd_of(number)

        @block.scalar
        def _(act):
            act.dma_start(resid[:, 0, :], x[0, 0:P, :]).then_inc(x_loaded, 16)
            act.dma_start(resid[:, 1, :], x[0, P:2 * P, :]).then_inc(x_loaded, 16)
            act.dma_start(ident[:, :], identity).then_inc(consts_loaded, 16)
            act.dma_start(mask[:, :], col_mask).then_inc(consts_loaded, 16)
            act.dma_start(pool_m[:, :, :, :], pool_matrix.rearrange("(k p) g q -> p k g q", p=P)
                          ).then_inc(consts_loaded, 16)

            def split_hi(slot, n, used=None, halves=(0, 1)):
                if 0 in halves:
                    act.wait_ge(raw_ready[slot], 32 * n + 32)
                    if used:
                        act.wait_ge(*used)
                for h in halves:
                    part = slice(h * HALF, (h + 1) * HALF)
                    nc.scalar.activation(w_hi[slot][:, part], w_raw[slot][:, part], ACT.Copy
                                         ).then_inc(hi_ready[slot], 1)

            def squares(number, t):
                act.wait_ge(resid_ready[t], number + 1)
                nc.scalar.activation(normed[:, t, :], resid[:, t, :], ACT.Square,
                                     scale=D_MODEL ** -0.5, accum_out=mean_sq[:, t:t + 1]).then_inc(sq_ready[t], 1)

            def norm(layer, number, late, early=None):
                def store_xt_hi(t):
                    for h in range(2):
                        act.wait_ge(xt_ready, number * 4 + (2 * t + h + 1))
                        nc.scalar.activation(xt_hi[:, t, 4 * h:4 * h + 4, :], ps[:, 6 + h, :],
                                             ACT.Copy).then_inc(xt_hi_ready, 1)

                squares(number, 0)
                if early:
                    split_hi(*early, used=(down_used, down_no(layer, FF1, 1)), halves=(0,))
                store_xt_hi(0)
                if early:
                    split_hi(*early, halves=(1,))
                squares(number, 1)
                split_hi(*late)
                store_xt_hi(1)

            def store_gt_hi(layer, ff, i, buf):
                act.wait_ge(gt_ready, chunk_no(layer, ff, i) + 1)
                nc.scalar.activation(gt_hi[:, buf, :, :, :], ps[:, 6, :], ACT.Copy
                                     ).then_inc(gt_hi_ready, 1)

            def silu_of(layer, ff, i, t):
                act.wait_ge(gu_ready[t], chunk_no(layer, ff, i) + 1)
                nc.scalar.activation(silu[:, t, :], ps[:, t, 0:FC], ACT.Silu
                                     ).then_inc(silu_ready[t], 1)

            def unit_g0(layer, ff, i):
                split_hi(ff["g"][0], unit_no(layer, ff["stage"], ff["g"][0], i),
                         used=(g0_used, chunk_no(layer, ff, i)))

            def unit_g1(layer, ff, i):
                split_hi(ff["g"][1], unit_no(layer, ff["stage"], ff["g"][1], i))

            def unit_down(layer, ff, i):
                split_hi(ff["d"], unit_no(layer, ff["stage"], ff["d"], i),
                         used=(down_used, down_no(layer, ff, i + 1)))

            def ff_stage(layer, ff, following=None):
                silu_of(layer, ff, 0, 0)
                unit_g0(layer, ff, 1)
                silu_of(layer, ff, 0, 1)
                unit_g1(layer, ff, 1)
                with act.Fori(1, LAST) as i:
                    unit_down(layer, ff, i - 1)
                    store_gt_hi(layer, ff, i - 1, 0)
                    silu_of(layer, ff, i, 0)
                    unit_g0(layer, ff, i + 1)
                    silu_of(layer, ff, i, 1)
                    unit_g1(layer, ff, i + 1)
                unit_down(layer, ff, LAST - 1)
                store_gt_hi(layer, ff, LAST - 1, 0)
                silu_of(layer, ff, LAST, 0)
                unit_g0(layer, ff, N_FF_CHUNKS)
                silu_of(layer, ff, LAST, 1)
                if following:
                    following()
                store_gt_hi(layer, ff, LAST, 1)

            def mix_number(layer, j):
                return unit_no(layer, 1, MIX_SLOTS[j], j // SLOTS)

            def mix_unit(layer, j):
                b = j - SLOTS
                if b < 0:
                    used = None
                elif b >= 8:
                    used = (w_out_used, layer * 3 + (b - 7))
                elif b % 2 == 0:
                    used = (z_used, layer * 4 + (b // 2 + 1))
                else:
                    used = (z_ready, layer * 8 + (b + 1))
                split_hi(MIX_SLOTS[j], mix_number(layer, j), used)

            def store_qv(layer, c, t):
                act.wait_ge(z_ready, layer * 8 + (2 * c + t + 1))
                nc.scalar.activation(z[:, t, c, :], ps[:, t, :], ACT.Copy,
                                     scale=HEAD_DIM ** -0.5 if c == 0 else 1.0
                                     ).then_inc(z_qv_stored, 1)

            def exps(layer, h):
                act.wait_ge(max_ready, layer * N_HEADS + (h + 1))
                for t in range(TT):
                    done = nc.scalar.activation(
                        scores[:, h % SCORE_BUFS, t, :], scores[:, h % SCORE_BUFS, t, :], ACT.Exp,
                        bias=neg_max[:, h, t:t + 1], accum_out=row_sum[:, t, h:h + 1])
                done.then_inc(probs_ready, 1)

            def store_probs_t(layer, h):
                act.wait_ge(probs_t_ready, layer * N_HEADS + (h + 1))
                nc.scalar.activation(probs_t[:, h % 2, :, :, :], ps[:, 6 + h % 2, :], ACT.Copy
                                     ).then_inc(probs_t_stored_a, 1)

            def mix_stage(layer):
                mix_unit(layer, 2)
                store_qv(layer, 0, 0)
                mix_unit(layer, 3)
                store_qv(layer, 0, 1)
                mix_unit(layer, 4)
                for h in range(2):
                    act.wait_ge(qk_t_ready, layer * 4 + (h + 1))
                    nc.scalar.activation(q_t[:, 2 * h:2 * h + 2, :, :], ps[:, 6 + h, :], ACT.Copy
                                         ).then_inc(q_t_stored, 1)
                mix_unit(layer, 5)
                store_qv(layer, 2, 0)
                mix_unit(layer, 6)
                store_qv(layer, 2, 1)
                exps(layer, 0)
                exps(layer, 1)
                mix_unit(layer, 7)
                exps(layer, 2)
                mix_unit(layer, 8)
                store_probs_t(layer, 0)
                exps(layer, 3)
                mix_unit(layer, 9)
                exps(layer, 4)
                store_probs_t(layer, 2)
                exps(layer, 5)
                exps(layer, 6)
                store_probs_t(layer, 4)
                exps(layer, 7)
                for g in range(N_GROUPS):
                    act.wait_ge(pooled_ready, layer * 2 + (g // 2 + 1))
                    nc.scalar.activation(
                        xt_hi[:, :, 4 + g, :],
                        ps[:, 2 + g // 2, (g % 2) * SEQ:(g % 2 + 1) * SEQ]
                        .rearrange("p (t q) -> p t q", t=TT),
                        ACT.Copy, scale=pool_scale_sb[:, g:g + 1]).then_inc(pooled_hi_ready, 1)
                store_probs_t(layer, 6)
                mix_unit(layer, 10)
                for t in range(TT):
                    act.wait_ge(heads_t_ready, layer * 2 + (t + 1))
                    nc.scalar.activation(xt_hi[:, t, 0:4, :], ps[:, 6 + t, :], ACT.Copy
                                         ).then_inc(heads_t_hi_ready, 1)
                mix_unit(layer, 11)
                split_hi(*first_unit(layer, FF2, 0), used=(w_out_used, layer * 3 + 2))

            with act.Fori(0, DEPTH) as layer:
                act.dma_start(gain[0][:, :], ffn1_norm[bass.ds(layer, 1), :].to_broadcast([P, D_MODEL])
                              ).then_inc(gain0_loaded, 16)
                act.dma_start(gain[1][:, :], mix_norm[bass.ds(layer, 1), :].to_broadcast([P, D_MODEL])
                              ).then_inc(params_loaded, 16)
                act.dma_start(gain[2][:, :], ffn2_norm[bass.ds(layer, 1), :].to_broadcast([P, D_MODEL])
                              ).then_inc(params_loaded, 16)
                act.dma_start(w_pool_sb[:, :, :],
                              w_pool[bass.ds(layer, 1), :, :, :].rearrange("o g c d -> c (o g) d")
                              ).then_inc(params_loaded, 16)
                with nc.allow_non_contiguous_dma(reason="512 words, once for each layer"):
                    act.dma_start(pool_scale_sb[:, :],
                                  pool_scale[bass.ds(layer, 1), :].rearrange("o (g c) -> c (o g)", c=P)
                                  ).then_inc(params_loaded, 16)
                norm(layer, layer * STAGES, first_unit(layer, FF1, 1), early=first_unit(layer, FF1, 0))
                act.wait_ge(bias_rows_loaded, 16 * DEPTH * 2 * N_HEADS)
                act.dma_start(bias[:, :, :, :].rearrange("p h d c -> p (h d c)"),
                              bias_dram[bass.ds(layer, 1), :, :].rearrange("o p e -> p (o e)")
                              ).then_inc(bias_loaded, 16)
                ff_stage(layer, FF1, following=lambda: mix_unit(layer, 0))
                norm(layer, layer * STAGES + 1, (MIX_SLOTS[1], mix_number(layer, 1)))
                mix_stage(layer)
                norm(layer, layer * STAGES + 2, first_unit(layer, FF2, 1))
                ff_stage(layer, FF2)
            act.dma_start(gain[0][:, :], final_norm.rearrange("(o n) -> o n", o=1).to_broadcast([P, D_MODEL])
                          ).then_inc(final_gain_loaded, 16)
            for t in range(TT):
                squares(STAGES * DEPTH, t)

        @block.vector
        def _(dve):
            nc.vector.memset(zeros[:, :].bitcast(F32), 0.0).then_inc(zeros_ready, 1)
            for slot in range(SLOTS):
                nc.vector.memset(seeds[:, slot:slot + 1], 0.0).then_inc(lo_ready[slot], 1)
            dve.wait_ge(x_loaded, 32)
            for t in range(TT):
                nc.vector.memset(seeds[:, SLOTS + t:SLOTS + t + 1], 0.0).then_inc(resid_ready[t], 1)

            def split_lo(slot, n, halves=(0, 1)):
                for h in halves:
                    part = slice(h * HALF, (h + 1) * HALF)
                    dve.wait_ge(hi_ready[slot], 2 * n + (h + 1))
                    nc.vector.tensor_tensor(w_lo[slot][:, part], w_raw[slot][:, part],
                                            w_hi[slot][:, part].bitcast(F32), ALU.subtract
                                            ).then_inc(lo_ready[slot], 1)

            def scale_rows(t, h, g):
                part = slice(h * 512, (h + 1) * 512)
                return nc.vector.scalar_tensor_tensor(
                    normed[:, t, part], resid[:, t, part], rstd[:, t:t + 1], gain[g][:, part],
                    ALU.mult, ALU.mult)

            def norm(layer, number, g, late, early=None, add=None):
                def rows(t):
                    dve.wait_ge(rstd_ready[t], number + 1)
                    for h in range(2):
                        scale_rows(t, h, g).then_inc(normed_ready, 1)

                def store_xt_lo(t):
                    for h in range(2):
                        dve.wait_ge(xt_hi_ready, number * 4 + (2 * t + h + 1))
                        nc.vector.tensor_tensor(
                            xt_lo[:, t, 4 * h:4 * h + 4, :],
                            ps[:, 6 + h, :].rearrange("p (k q) -> p k q", k=4),
                            xt_hi[:, t, 4 * h:4 * h + 4, :].bitcast(F32), ALU.subtract
                        ).then_inc(xt_lo_ready, 1)

                if add:
                    add(0)
                rows(0)
                if early:
                    split_lo(*early, halves=(0,))
                store_xt_lo(0)
                if early:
                    split_lo(*early, halves=(1,))
                if add:
                    add(1)
                split_lo(*late, halves=(0,))
                rows(1)
                split_lo(*late, halves=(1,))
                store_xt_lo(1)

            def gate(layer, ff, i, t):
                dve.wait_ge(silu_ready[t], chunk_no(layer, ff, i) + 1)
                nc.vector.scalar_tensor_tensor(gated[:, t, :], ps[:, t, FC:2 * FC], 0.5,
                                               silu[:, t, :], ALU.mult, ALU.mult
                                               ).then_inc(gated_ready[t], 1)

            def store_gt_lo(layer, ff, i, buf):
                dve.wait_ge(gt_hi_ready, chunk_no(layer, ff, i) + 1)
                nc.vector.tensor_tensor(
                    gt_lo[:, buf, :, :, :].rearrange("p k t q -> p (k t q)"), ps[:, 6, :],
                    gt_hi[:, buf, :, :, :].rearrange("p k t q -> p (k t q)").bitcast(F32),
                    ALU.subtract).then_inc(gt_lo_ready, 1)

            def unit(layer, ff, slot, k):
                split_lo(slot, unit_no(layer, ff["stage"], slot, k))

            def add_to_residual(layer, stage, t):
                dve.wait_ge(acc_ready[t], layer * STAGES + (stage + 1))
                nc.vector.tensor_tensor(resid[:, t, :], ps[:, 2 + 2 * t:4 + 2 * t, :]
                                        .rearrange("p b c -> p (b c)"), resid[:, t, :], ALU.add
                                        ).then_inc(resid_ready[t], 1)

            def ff_stage(layer, ff, following=None):
                g0, g1 = ff["g"]
                gate(layer, ff, 0, 0)
                unit(layer, ff, g0, 1)
                gate(layer, ff, 0, 1)
                unit(layer, ff, g1, 1)
                with dve.Fori(1, LAST) as i:
                    unit(layer, ff, ff["d"], i - 1)
                    store_gt_lo(layer, ff, i - 1, 0)
                    gate(layer, ff, i, 0)
                    unit(layer, ff, g0, i + 1)
                    gate(layer, ff, i, 1)
                    unit(layer, ff, g1, i + 1)
                unit(layer, ff, ff["d"], LAST - 1)
                store_gt_lo(layer, ff, LAST - 1, 0)
                gate(layer, ff, LAST, 0)
                unit(layer, ff, g0, N_FF_CHUNKS)
                gate(layer, ff, LAST, 1)
                if following:
                    following()
                store_gt_lo(layer, ff, LAST, 1)

            def mix_number(layer, j):
                return unit_no(layer, 1, MIX_SLOTS[j], j // SLOTS)

            def mix_unit(layer, j):
                split_lo(MIX_SLOTS[j], mix_number(layer, j))

            def store_kp(layer, c, t):
                dve.wait_ge(z_ready, layer * 8 + (2 * c + t + 1))
                nc.vector.tensor_copy(z[:, t, c, :], ps[:, 2 + t, :]).then_inc(z_kp_stored, 1)

            def add_bias(layer, h):
                dve.wait_ge(scores_ready, layer * N_HEADS + (h + 1))
                if h >= SCORE_BUFS:
                    dve.wait_ge(probs_t_ready, layer * N_HEADS + (h - SCORE_BUFS + 1))
                nc.vector.memset(wait_mark[:, :], 0.0)
                for t in range(TT):
                    done = nc.vector.tensor_tensor_reduce(
                        out=scores[:, h % SCORE_BUFS, t, :], in0=ps[:, 4 + h % 2, t * SEQ:(t + 1) * SEQ],
                        in1=bias[:, h, 2 - 2 * t:2 - 2 * t + ROWS, :].rearrange("p d c -> p (d c)"),
                        scale=1.0, scalar=-3.0e38, op0=ALU.add, op1=ALU.max,
                        accum_out=row_max[:, h, t:t + 1])
                done.then_inc(biased_ready, 1)
                dve.wait_ge(biased_ready, layer * N_HEADS + (h + 1))
                nc.vector.tensor_scalar(neg_max[:, h, :], row_max[:, h, :], -1.0, None, ALU.mult
                                        ).then_inc(max_ready, 1)

            def store_probs_t(layer, h):
                dve.wait_ge(probs_t_ready, layer * N_HEADS + (h + 1))
                nc.vector.tensor_copy(
                    probs_t[:, h % 2, :, :, :].rearrange("p k t q -> p (k t q)"),
                    ps[:, 6 + h % 2, :]).then_inc(probs_t_stored_v, 1)

            def mix_stage(layer):
                mix_unit(layer, 2)
                dve.wait_ge(bias_loaded, layer * 16 + 16)
                for h in range(0, N_HEADS, 2):
                    done = nc.vector.tensor_tensor(
                        bias[:, h:h + 2, :, :].rearrange("p h d c -> p (h d) c"),
                        bias[:, h:h + 2, :, :].rearrange("p h d c -> p (h d) c"),
                        mask[:, :].rearrange("p (o c) -> p o c", o=1).to_broadcast([P, 2 * DELTAS, GRID_W]),
                        ALU.min)
                done.then_inc(bias_masked, 1)
                mix_unit(layer, 3)
                mix_unit(layer, 4)
                store_kp(layer, 1, 0)
                mix_unit(layer, 5)
                store_kp(layer, 1, 1)
                for h in range(2):
                    dve.wait_ge(qk_t_ready, layer * 4 + (h + 3))
                    nc.vector.tensor_copy(
                        k_t[:, 2 * h:2 * h + 2, :, :].rearrange("p g t q -> p (g t q)"),
                        ps[:, 6 + h, :]).then_inc(k_t_stored, 1)
                dve.wait_ge(bias_masked, layer + 1)
                mix_unit(layer, 6)
                add_bias(layer, 0)
                add_bias(layer, 1)
                mix_unit(layer, 7)
                add_bias(layer, 2)
                store_kp(layer, 3, 0)
                mix_unit(layer, 8)
                add_bias(layer, 3)
                mix_unit(layer, 9)
                store_kp(layer, 3, 1)
                add_bias(layer, 4)
                store_probs_t(layer, 1)
                add_bias(layer, 5)
                for j in range(2):
                    dve.wait_ge(diff_ready, layer * 2 + (j + 1))
                    nc.vector.tensor_copy(z[:, j, 1, :], ps[:, 2 + j, :]).then_inc(diff_stored, 1)
                add_bias(layer, 6)
                store_probs_t(layer, 3)
                add_bias(layer, 7)
                for g in range(N_GROUPS):
                    if g % 2 == 0:
                        dve.wait_ge(pooled_hi_ready, layer * N_GROUPS + (g + 2))
                    nc.vector.scalar_tensor_tensor(
                        xt_lo[:, :, 4 + g, :],
                        ps[:, 2 + g // 2, (g % 2) * SEQ:(g % 2 + 1) * SEQ]
                        .rearrange("p (t q) -> p t q", t=TT),
                        pool_scale_sb[:, g:g + 1], xt_hi[:, :, 4 + g, :].bitcast(F32),
                        ALU.mult, ALU.subtract).then_inc(pooled_lo_ready, 1)
                store_probs_t(layer, 5)
                store_probs_t(layer, 7)
                dve.wait_ge(probs_ready, layer * N_HEADS + N_HEADS)
                nc.vector.reciprocal(inv_sum[:, :, :], row_sum[:, :, :]).then_inc(inv_ready, 1)
                mix_unit(layer, 10)
                dve.wait_ge(inv_ready, layer + 1)
                dve.wait_ge(pv_ready, layer * N_HEADS + N_HEADS)
                for t in range(TT):
                    nc.vector.tensor_tensor(
                        heads_out(t).rearrange("p (h d) -> p h d", h=N_HEADS),
                        ps[:, t, :].rearrange("p (h d) -> p h d", h=N_HEADS),
                        inv_sum[:, t, :].rearrange("p (h o) -> p h o", o=1)
                        .to_broadcast([P, N_HEADS, HEAD_DIM]), ALU.mult).then_inc(heads_stored, 1)
                for t in range(TT):
                    dve.wait_ge(heads_t_hi_ready, layer * 2 + (t + 1))
                    nc.vector.tensor_tensor(
                        xt_lo[:, t, 0:4, :], ps[:, 6 + t, :].rearrange("p (k q) -> p k q", k=4),
                        xt_hi[:, t, 0:4, :].bitcast(F32), ALU.subtract
                    ).then_inc(heads_t_lo_ready, 1)
                mix_unit(layer, 11)
                unit(layer, FF2, FF2["g"][0], 0)

            dve.wait_ge(consts_loaded, 48)
            with dve.Fori(0, DEPTH) as layer:
                dve.wait_ge(gain0_loaded, layer * 16 + 16)
                norm(layer, layer * STAGES, 0, first_unit(layer, FF1, 1), early=first_unit(layer, FF1, 0))
                ff_stage(layer, FF1, following=lambda: mix_unit(layer, 0))
                dve.wait_ge(params_loaded, layer * 64 + 64)
                norm(layer, layer * STAGES + 1, 1, (MIX_SLOTS[1], mix_number(layer, 1)),
                     add=lambda t: add_to_residual(layer, 0, t))
                mix_stage(layer)
                norm(layer, layer * STAGES + 2, 2, first_unit(layer, FF2, 1),
                     add=lambda t: add_to_residual(layer, 1, t))
                ff_stage(layer, FF2)
                for t in range(TT):
                    add_to_residual(layer, 2, t)
            dve.wait_ge(final_gain_loaded, 16)
            for t in range(TT):
                dve.wait_ge(rstd_ready[t], STAGES * DEPTH + 1)
                for h in range(2):
                    done = scale_rows(t, h, 0)
                done.then_inc(out_ready, 1)

        @block.tensor
        def _(pe):
            def split_products(outs, hi, lo, w_his, w_los, start, stop):
                for o, wh, wl in zip(outs, w_his, w_los):
                    nc.tensor.matmul(o, hi, wh, start=start, stop=False)
                    nc.tensor.matmul(o, hi, wl, start=False, stop=False)
                for o, wh in zip(outs, w_his):
                    last = nc.tensor.matmul(o, lo, wh, start=False, stop=stop)
                return last

            def wait_split(slot, n, h):
                pe.wait_ge(lo_ready[slot], 2 * n + (h + 2))

            def project_in(bank, t, slots, numbers, used, on_half=None):
                for kt in range(KT):
                    a, k = kt // 4, kt % 4
                    slot = slots[a]
                    if t == 0 and k % 2 == 0:
                        wait_split(slot, numbers[a], k // 2)
                    if on_half is not None and k == 0:
                        on_half(a)
                    cols = slice(k * BANK, (k + 1) * BANK)
                    last = split_products([ps[:, bank, :]], xt_hi[:, t, kt, :], xt_lo[:, t, kt, :],
                                          [w_hi[slot][:, cols]], [w_lo[slot][:, cols]],
                                          kt == 0, kt == KT - 1)
                    if t == TT - 1 and k == 3 and a == 0:
                        last.then_inc(used, 1)
                return last

            def into_acc(t, slot, number, kt, hi, lo, wait, start=False, stop=False):
                if wait:
                    wait_split(slot, number, kt)
                cols = [slice(kt * HALF + dh * BANK, kt * HALF + (dh + 1) * BANK) for dh in range(2)]
                return split_products([acc(t, dh) for dh in range(2)], hi, lo,
                                      [w_hi[slot][:, c] for c in cols],
                                      [w_lo[slot][:, c] for c in cols], start, stop)

            def clear_acc(t):
                for dh in range(2):
                    nc.tensor.matmul(acc(t, dh), zeros[:, 0:P], zeros[:, :], start=True, stop=False)

            def transpose_normed(number, t):
                for h in range(2):
                    pe.wait_ge(normed_ready, number * 4 + (2 * t + h + 1))
                    if t == 1:
                        pe.wait_ge(xt_lo_ready, number * 4 + (h + 1))
                    for k in range(4):
                        c = (4 * h + k) * P
                        last = nc.tensor.transpose(ps[:, 6 + h, k * P:(k + 1) * P],
                                                   normed[:, t, c:c + P], ident[:, :])
                    last.then_inc(xt_ready, 1)

            def gate_up(layer, ff, i, t, on_half=None):
                numbers = [unit_no(layer, ff["stage"], s, i) for s in ff["g"]]
                return project_in(t, t, ff["g"], numbers, g0_used, on_half)

            def transpose_gated(layer, ff, i):
                for t in range(TT):
                    pe.wait_ge(gated_ready[t], chunk_no(layer, ff, i) + 1)
                    for k in range(2):
                        last = nc.tensor.transpose(ps[:, 6, (k * TT + t) * P:(k * TT + t + 1) * P],
                                                   gated[:, t, k * P:(k + 1) * P], ident[:, :])
                last.then_inc(gt_ready, 1)

            def down(layer, ff, i, t, k, slot, number, buf, wait, stop=False):
                if wait:
                    pe.wait_ge(gt_lo_ready, chunk_no(layer, ff, i) + 1)
                return into_acc(t, slot, number, k, gt_hi[:, buf, k, t, :], gt_lo[:, buf, k, t, :],
                                wait, stop=stop)

            def norm_then_first(number, first):
                transpose_normed(number, 0)

                def on_half(a):
                    pe.wait_ge(xt_lo_ready, number * 4 + (a + 1))
                    if a == 1:
                        transpose_normed(number, 1)

                first(on_half)
                pe.wait_ge(xt_lo_ready, number * 4 + 4)

            def ff_stage(layer, ff):
                d = ff["d"]
                norm_then_first(layer * STAGES + ff["stage"],
                                lambda on_half: gate_up(layer, ff, 0, 0, on_half)
                                .then_inc(gu_ready[0], 1))
                for t in range(TT):
                    clear_acc(t)
                gate_up(layer, ff, 0, 1).then_inc(gu_ready[1], 1)
                with pe.Fori(1, LAST) as i:
                    for t in range(TT):
                        pe.wait_ge(gated_ready[t], chunk_no(layer, ff, i))
                        gate_up(layer, ff, i, t).then_inc(gu_ready[t], 1)
                        if t == 0:
                            transpose_gated(layer, ff, i - 1)
                    n = unit_no(layer, ff["stage"], d, i - 1)
                    for t in range(TT):
                        for k in range(2):
                            last = down(layer, ff, i - 1, t, k, d, n, 0, t == 0)
                    last.then_inc(down_used, 1)
                for t in range(TT):
                    pe.wait_ge(gated_ready[t], chunk_no(layer, ff, LAST))
                    gate_up(layer, ff, LAST, t).then_inc(gu_ready[t], 1)
                    if t == 0:
                        transpose_gated(layer, ff, LAST - 1)
                n = unit_no(layer, ff["stage"], d, LAST - 1)
                m = unit_no(layer, ff["stage"], ff["g"][0], N_FF_CHUNKS)
                down(layer, ff, LAST - 1, 0, 0, d, n, 0, True)
                down(layer, ff, LAST - 1, 0, 1, d, n, 0, True)
                transpose_gated(layer, ff, LAST)
                down(layer, ff, LAST - 1, 1, 0, d, n, 0, False)
                down(layer, ff, LAST, 0, 0, ff["g"][0], m, 1, True)
                down(layer, ff, LAST, 0, 1, ff["g"][0], m, 1, True, stop=True
                     ).then_inc(acc_ready[0], 1)
                down(layer, ff, LAST - 1, 1, 1, d, n, 0, False).then_inc(down_used, 1)
                down(layer, ff, LAST, 1, 0, ff["g"][0], m, 1, False)
                down(layer, ff, LAST, 1, 1, ff["g"][0], m, 1, False, stop=True
                     ).then_inc(acc_ready[1], 1)

            def mix_number(layer, j):
                return unit_no(layer, 1, MIX_SLOTS[j], j // SLOTS)

            def project_z(layer, c, t, on_half=None):
                slots = MIX_SLOTS[2 * c:2 * c + 2]
                numbers = [mix_number(layer, 2 * c + a) for a in range(2)]
                project_in(t + 2 * (c % 2), t, slots, numbers, z_used, on_half
                           ).then_inc(z_ready, 1)

            def transpose_heads(layer, c, h):
                for g in range(2):
                    for t in range(TT):
                        col = (2 * h + g) * P
                        last = nc.tensor.transpose(
                            ps[:, 6 + h, (g * TT + t) * P:(g * TT + t + 1) * P],
                            z[:, t, c, col:col + P], ident[:, :])
                last.then_inc(qk_t_ready, 1)

            def head_scores(layer, h):
                if h >= 2:
                    pe.wait_ge(biased_ready, layer * N_HEADS + (h - 1))
                rows = slice((h % 2) * HEAD_DIM, (h % 2 + 1) * HEAD_DIM)
                for t in range(TT):
                    last = nc.tensor.matmul(ps[:, 4 + h % 2, t * SEQ:(t + 1) * SEQ],
                                            q_t[rows, h // 2, t, :], k_t[rows, h // 2, :, :],
                                            start=True, stop=True)
                last.then_inc(scores_ready, 1)

            def wait_probs_t_stored(layer, h):
                if h % 2 == 0:
                    pe.wait_ge(probs_t_stored_a, layer * (N_HEADS // 2) + (h // 2 + 1))
                else:
                    pe.wait_ge(probs_t_stored_v, layer * (N_HEADS // 2) + (h // 2 + 1))

            def transpose_probs(layer, h):
                pe.wait_ge(probs_ready, layer * N_HEADS + (h + 1))
                if h >= 2:
                    wait_probs_t_stored(layer, h - 2)
                for k in range(TT):
                    for t in range(TT):
                        last = nc.tensor.transpose(
                            ps[:, 6 + h % 2, (k * TT + t) * P:(k * TT + t + 1) * P],
                            scores[:, h % SCORE_BUFS, t, k * P:(k + 1) * P], ident[:, :])
                last.then_inc(probs_t_ready, 1)

            def probs_v(layer, h):
                wait_probs_t_stored(layer, h)
                for t in range(TT):
                    for k in range(TT):
                        last = nc.tensor.matmul(
                            ps[:, t, h * HEAD_DIM:(h + 1) * HEAD_DIM], probs_t[:, h % 2, k, t, :],
                            z[:, k, 2, h * HEAD_DIM:(h + 1) * HEAD_DIM],
                            start=(k == 0), stop=(k == TT - 1))
                last.then_inc(pv_ready, 1)

            def pool_differences(layer):
                pe.wait_ge(z_kp_stored, layer * 4 + 4)
                for g in range(N_GROUPS):
                    for k in range(TT):
                        last = nc.tensor.matmul(
                            ps[:, 2 + g // 2, (g % 2) * SEQ:(g % 2 + 1) * SEQ],
                            z[:, k, 3, g * P:(g + 1) * P], pool_m[:, k, g, :],
                            start=(k == 0), stop=(k == TT - 1))
                    if g % 2 == 1:
                        last.then_inc(diff_ready, 1)

            def pool_linear(layer):
                for g in range(N_GROUPS):
                    if g % 2 == 0:
                        pe.wait_ge(diff_stored, layer * 2 + (g // 2 + 1))
                    last = nc.tensor.matmul(
                        ps[:, 2 + g // 2, (g % 2) * SEQ:(g % 2 + 1) * SEQ],
                        w_pool_sb[:, g, :], diff_t(g), start=True, stop=True)
                    if g % 2 == 1:
                        last.then_inc(pooled_ready, 1)

            def out_tile(layer, t, j, k, wait, start=False, stop=False):
                kt = (4, 6, 0, 2)[j - 8] + k
                return into_acc(t, MIX_SLOTS[j], mix_number(layer, j), k, xt_hi[:, t, kt, :],
                                xt_lo[:, t, kt, :], wait, start, stop)

            def mix_stage(layer):
                norm_then_first(layer * STAGES + 1,
                                lambda on_half: project_z(layer, 0, 0, on_half))
                project_z(layer, 0, 1)
                project_z(layer, 1, 0)
                pe.wait_ge(z_qv_stored, layer * 4 + 2)
                for h in range(2):
                    transpose_heads(layer, 0, h)
                project_z(layer, 1, 1)
                project_z(layer, 2, 0)
                pe.wait_ge(z_kp_stored, layer * 4 + 2)
                for h in range(2):
                    pe.wait_ge(q_t_stored, layer * 2 + (h + 1))
                    transpose_heads(layer, 1, h)
                project_z(layer, 2, 1)
                pe.wait_ge(k_t_stored, layer * 2 + 2)
                head_scores(layer, 0)
                head_scores(layer, 1)
                project_z(layer, 3, 0)
                head_scores(layer, 2)
                transpose_probs(layer, 0)
                project_z(layer, 3, 1)
                head_scores(layer, 3)
                pe.wait_ge(z_qv_stored, layer * 4 + 4)
                probs_v(layer, 0)
                transpose_probs(layer, 1)
                head_scores(layer, 4)
                transpose_probs(layer, 2)
                probs_v(layer, 1)
                head_scores(layer, 5)
                pool_differences(layer)
                probs_v(layer, 2)
                transpose_probs(layer, 3)
                head_scores(layer, 6)
                transpose_probs(layer, 4)
                probs_v(layer, 3)
                head_scores(layer, 7)
                pe.wait_ge(params_loaded, layer * 64 + 64)
                pool_linear(layer)
                probs_v(layer, 4)
                transpose_probs(layer, 5)
                transpose_probs(layer, 6)
                pe.wait_ge(pooled_lo_ready, layer * N_GROUPS + N_GROUPS)
                out_tile(layer, 0, 8, 0, True, start=True)
                out_tile(layer, 0, 8, 1, True)
                probs_v(layer, 5)
                transpose_probs(layer, 7)
                out_tile(layer, 0, 9, 0, True)
                out_tile(layer, 0, 9, 1, True)
                probs_v(layer, 6)
                probs_v(layer, 7)
                pe.wait_ge(biased_ready, layer * N_HEADS + N_HEADS)
                out_tile(layer, 1, 8, 0, False, start=True)
                out_tile(layer, 1, 8, 1, False).then_inc(w_out_used, 1)
                out_tile(layer, 1, 9, 0, False)
                out_tile(layer, 1, 9, 1, False).then_inc(w_out_used, 1)
                for t in range(TT):
                    pe.wait_ge(heads_stored, layer * 2 + (t + 1))
                    for k in range(4):
                        last = nc.tensor.transpose(ps[:, 6 + t, k * P:(k + 1) * P],
                                                   heads_out(t)[:, k * P:(k + 1) * P], ident[:, :])
                    last.then_inc(heads_t_ready, 1)
                for t in range(TT):
                    pe.wait_ge(heads_t_lo_ready, layer * 2 + (t + 1))
                    for j in (10, 11):
                        for k in range(2):
                            last = out_tile(layer, t, j, k, t == 0, stop=(j == 11 and k == 1))
                        if j == 10 and t == 1:
                            last.then_inc(w_out_used, 1)
                    last.then_inc(acc_ready[t], 1)

            pe.wait_ge(zeros_ready, 1)
            nc.tensor.matmul(ps[:, 0, :], zeros[:, 0:P], zeros[:, :], start=True, stop=True
                             ).then_inc(down_used, 1)
            pe.wait_ge(consts_loaded, 48)
            with pe.Fori(0, DEPTH) as layer:
                ff_stage(layer, FF1)
                mix_stage(layer)
                ff_stage(layer, FF2)


_INS = ["x", "ffn1_norm", "ffn1_w_gate", "ffn1_w_up", "ffn1_w_down", "mix_norm", "w_in", "rpb",
        "w_pool", "pool_scale", "w_out", "ffn2_norm", "ffn2_w_gate", "ffn2_w_up", "ffn2_w_down",
        "final_norm"]


def _constants():
    import numpy as np

    identity = np.eye(P, dtype=np.float32)
    cols = np.arange(GRID_W)
    start = np.clip(cols - WIN_COLS // 2, 0, GRID_W - WIN_COLS)
    inside = (cols[None, :] >= start[:, None]) & (cols[None, :] < start[:, None] + WIN_COLS)
    col_mask = np.where(inside, np.float32(3.4e38), np.float32(-1e30)).astype(np.float32)
    col_mask = np.tile(col_mask, (P // GRID_W, 1))
    t = np.arange(SEQ)
    pool_matrix = np.zeros((SEQ, N_GROUPS, SEQ), np.float64)
    for g, w in enumerate(POOL_WINDOWS):
        lo, hi = np.clip(t - w // 2, 0, SEQ), np.clip(t - w // 2 + w, 0, SEQ)
        window = (t[:, None] >= lo[None, :]) & (t[:, None] < hi[None, :])
        pool_matrix[:, g, :] = window / (hi - lo)[None, :] - np.eye(SEQ)
    return {"identity": identity, "col_mask": col_mask, "pool_matrix": pool_matrix.astype(np.float32)}


def kernel(**inputs):
    import numpy as _np
    import concourse.bacc as _bacc
    from concourse.bass_utils import run_bass_kernel_spmd as _run

    nc = _bacc.Bacc("TRN2", target_bir_lowering=False, num_devices=1)
    arrays, args = {}, []
    named = {name: _np.ascontiguousarray(inputs[name]) for name in _INS}
    named.update(_constants())
    for name, a in named.items():
        arrays[f"in_{name}_dram"] = a
        args.append(nc.dram_tensor(f"in_{name}_dram", a.shape, mybir.dt.from_np(a.dtype),
                                   kind="ExternalInput").ap())
    args.append(nc.dram_tensor("out_0_dram", (1, SEQ, D_MODEL), mybir.dt.float32,
                               kind="ExternalOutput").ap())
    trunk(nc, *args)
    r = _run(nc, [arrays], core_ids=[0])
    return r.results[0]["out_0_dram"]
```
